# Optimizing a Trainium2 kernel written in Bass

```python
import jax, jax.numpy as jnp
from jax import lax
import numpy as np

D_MODEL = 1024
BATCH = 1
SEQ = 256
DEPTH = 2
DEC_BATCH = 1
DEC_SEQ = 1024
PAST_LEN = 512

GRID_W = 64
MLA_HEADS = 4
QK_NOPE = 128
QK_ROPE = 64
V_HEAD = 128
Q_RANK = 256
KV_RANK = 128
MLA_WIDTH = MLA_HEADS * V_HEAD
CONV_GROUPS = 4
CONV_WIDTH = 256
CONV_K = 3
CMLP_GROUPS = 4
CMLP_WIDTH = 256
CHUNK = 128
MIX_WIDTH = MLA_WIDTH + CONV_WIDTH + CMLP_WIDTH
IN_WIDTH = Q_RANK + KV_RANK + QK_ROPE + 3 * CONV_WIDTH + 2 * CMLP_WIDTH
N_EXPERTS = 16
EC_FACTOR = 2
EXPERT_FF = D_MODEL // 2
ROPE_BASE = 10000.0
EPS = 1e-6
Q_BLOCK = 128

kernel_name = "hybrid_mla_conv_gmlp_ec_diffusion_step"

def rmsnorm(x, g):
    xf = x.astype(jnp.float32)
    y = xf * lax.rsqrt(jnp.mean(xf * xf, axis=-1, keepdims=True) + EPS)
    return (y * g.astype(jnp.float32)).astype(x.dtype)

def axial_rope_tables(n_tokens, dtype):
    rows = n_tokens // GRID_W
    row = jnp.repeat(jnp.arange(rows), GRID_W).astype(jnp.float32)
    col = jnp.tile(jnp.arange(GRID_W), rows).astype(jnp.float32)
    n_freq = QK_ROPE // 4
    inv = ROPE_BASE ** (-jnp.arange(n_freq, dtype=jnp.float32) / n_freq)
    ang_r = row[:, None] * inv
    ang_c = col[:, None] * inv
    ang = jnp.concatenate([ang_r, ang_r, ang_c, ang_c], axis=-1)
    return jnp.cos(ang).astype(dtype), jnp.sin(ang).astype(dtype)

def apply_axial_rope(x, cos, sin):
    x1, x2, x3, x4 = jnp.split(x, 4, axis=-1)
    rot = jnp.concatenate([-x2, x1, -x4, x3], axis=-1)
    return x * cos + rot * sin

def block_attention(q, k, v):
    b, lq, h, dk = q.shape
    nb = lq // Q_BLOCK
    qb = q.reshape(b, nb, Q_BLOCK, h, dk).transpose(1, 0, 2, 3, 4)
    scale = dk ** -0.5

    def one_block(qi):
        s = jnp.einsum('bqhd,bkhd->bhqk', qi, k).astype(jnp.float32) * scale
        p = jax.nn.softmax(s, axis=-1).astype(v.dtype)
        return jnp.einsum('bhqk,bkhd->bqhd', p, v)

    o = lax.map(one_block, qb)
    return o.transpose(1, 0, 2, 3, 4).reshape(b, lq, h, v.shape[-1])

def token_mixers(h, rope, ctx_ckv, ctx_krope, p):
    b, n, _ = h.shape
    proj = h @ p['w_in']
    offs = [Q_RANK, Q_RANK + KV_RANK, Q_RANK + KV_RANK + QK_ROPE,
            Q_RANK + KV_RANK + QK_ROPE + 3 * CONV_WIDTH]
    c_q, c_kv, k_pe, conv_in, cmlp_in = jnp.split(proj, offs, axis=-1)

    q = (rmsnorm(c_q, p['q_norm_g']) @ p['w_uq']).reshape(b, n, MLA_HEADS, QK_NOPE + QK_ROPE)
    q_nope, q_pe = q[..., :QK_NOPE], q[..., QK_NOPE:]
    c_kv = rmsnorm(c_kv, p['kv_norm_g'])
    if rope is None:
        all_ckv, all_kpe = c_kv, k_pe
    else:
        cos, sin = rope
        q_pe = apply_axial_rope(q_pe, cos[:, None, :], sin[:, None, :])
        k_pe_rot = apply_axial_rope(k_pe, cos, sin)
        all_ckv = jnp.concatenate([ctx_ckv, c_kv], axis=1)
        all_kpe = jnp.concatenate([ctx_krope, k_pe_rot], axis=1)
    lk = all_ckv.shape[1]
    kv = (all_ckv @ p['w_ukv']).reshape(b, lk, MLA_HEADS, QK_NOPE + V_HEAD)
    k_nope, v = kv[..., :QK_NOPE], kv[..., QK_NOPE:]
    k = jnp.concatenate(
        [k_nope, jnp.broadcast_to(all_kpe[:, :, None, :], (b, lk, MLA_HEADS, QK_ROPE))], axis=-1)
    qf = jnp.concatenate([q_nope, q_pe], axis=-1)
    attn_out = block_attention(qf, k, v).reshape(b, n, MLA_WIDTH)

    g_b, g_c, xc = jnp.split(conv_in, 3, axis=-1)
    z = jnp.pad(g_c * xc, ((0, 0), (1, 1), (0, 0)))
    cw = p['conv_w']
    conv = z[:, :-2] * cw[0] + z[:, 1:-1] * cw[1] + z[:, 2:] * cw[2]
    conv_out = g_b * conv

    u, vv = jnp.split(cmlp_in, 2, axis=-1)
    nc = n // CHUNK
    vg = vv.reshape(b, nc, CHUNK, CMLP_GROUPS, CMLP_WIDTH // CMLP_GROUPS)
    mixed = (jnp.einsum('gpq,bcqgd->bcpgd', p['spatial_w'], vg)
             + p['spatial_b'].T[:, :, None])
    cmlp_out = u * mixed.reshape(b, n, CMLP_WIDTH)

    out = jnp.concatenate([attn_out, conv_out, cmlp_out], axis=-1) @ p['w_out']
    return out, c_kv, k_pe

def expert_choice_ffn(h, p):
    b, n, d = h.shape
    cap = (EC_FACTOR * n) // N_EXPERTS
    logits = jnp.einsum('bnd,de->bne', h, p['w_router']).astype(jnp.float32)
    aff = jax.nn.softmax(logits, axis=-1)
    gates, idx = lax.top_k(aff.transpose(0, 2, 1), cap)
    xs = jax.vmap(lambda hb, ib: hb[ib])(h, idx)
    hid = (jax.nn.silu(jnp.einsum('becd,edf->becf', xs, p['w_gate']))
           * jnp.einsum('becd,edf->becf', xs, p['w_up']))
    ye = jnp.einsum('becf,efd->becd', hid, p['w_down']) * gates[..., None].astype(h.dtype)
    flat = (idx + (jnp.arange(b) * n)[:, None, None]).reshape(-1)
    out = jnp.zeros((b * n, d), h.dtype).at[flat].add(ye.reshape(-1, d))
    return out.reshape(b, n, d)

def layer_step(x, mod, rope, ctx_ckv, ctx_krope, p):
    sh1, sc1, g1, sh2, sc2, g2 = jnp.split(mod, 6, axis=-1)
    h = rmsnorm(x, p['norm1_g']) * (1 + sc1) + sh1
    mix, ckv, kpe = token_mixers(h, rope, ctx_ckv, ctx_krope, p)
    x = x + g1 * mix
    h = rmsnorm(x, p['norm2_g']) * (1 + sc2) + sh2
    x = x + g2 * expert_choice_ffn(h, p)
    return x, ckv, kpe

def setup_inputs(seed: int = 0) -> dict:
    key = jax.random.key(seed)
    ks = jax.random.split(key, 26)
    f32 = jnp.float32

    def nrm(k, shape, scale):
        return jax.random.normal(k, shape, f32) * scale

    return {
        "x_prompt": nrm(ks[0], (BATCH, SEQ, D_MODEL), 1.0),
        "x_sample": nrm(ks[1], (DEC_BATCH, DEC_SEQ, D_MODEL), 1.0),
        "cache_ckv": nrm(ks[2], (DEC_BATCH, DEPTH, PAST_LEN, KV_RANK), 1.0),
        "cache_krope": nrm(ks[3], (DEC_BATCH, DEPTH, PAST_LEN, QK_ROPE), 1.0),
        "c": nrm(ks[4], (DEC_BATCH, D_MODEL), 1.0),
        "c_ctx": nrm(ks[5], (D_MODEL,), 1.0),
        "w_ada": nrm(ks[6], (DEPTH, D_MODEL, 6 * D_MODEL), 0.5 * D_MODEL ** -0.5),
        "b_ada": nrm(ks[7], (DEPTH, 6 * D_MODEL), 0.02),
        "norm1_g": 1.0 + nrm(ks[8], (DEPTH, D_MODEL), 0.05),
        "norm2_g": 1.0 + nrm(ks[9], (DEPTH, D_MODEL), 0.05),
        "w_in": nrm(ks[10], (DEPTH, D_MODEL, IN_WIDTH), D_MODEL ** -0.5),
        "q_norm_g": 1.0 + nrm(ks[11], (DEPTH, Q_RANK), 0.05),
        "kv_norm_g": 1.0 + nrm(ks[12], (DEPTH, KV_RANK), 0.05),
        "w_uq": nrm(ks[13], (DEPTH, Q_RANK, MLA_HEADS * (QK_NOPE + QK_ROPE)), Q_RANK ** -0.5),
        "w_ukv": nrm(ks[14], (DEPTH, KV_RANK, MLA_HEADS * (QK_NOPE + V_HEAD)), KV_RANK ** -0.5),
        "conv_w": nrm(ks[15], (DEPTH, CONV_K, CONV_WIDTH), CONV_K ** -0.5),
        "spatial_w": nrm(ks[16], (DEPTH, CMLP_GROUPS, CHUNK, CHUNK), CHUNK ** -0.5),
        "spatial_b": 1.0 + nrm(ks[17], (DEPTH, CMLP_GROUPS, CHUNK), 0.1),
        "w_out": nrm(ks[18], (DEPTH, MIX_WIDTH, D_MODEL), MIX_WIDTH ** -0.5),
        "w_router": nrm(ks[19], (DEPTH, D_MODEL, N_EXPERTS), D_MODEL ** -0.5),
        "w_gate": nrm(ks[20], (DEPTH, N_EXPERTS, D_MODEL, EXPERT_FF), D_MODEL ** -0.5),
        "w_up": nrm(ks[21], (DEPTH, N_EXPERTS, D_MODEL, EXPERT_FF), D_MODEL ** -0.5),
        "w_down": nrm(ks[22], (DEPTH, N_EXPERTS, EXPERT_FF, D_MODEL), EXPERT_FF ** -0.5),
        "final_norm_g": 1.0 + nrm(ks[23], (D_MODEL,), 0.05),
    }

def reference(x_prompt, x_sample, cache_ckv, cache_krope, c, c_ctx, w_ada, b_ada,
              norm1_g, norm2_g, w_in, q_norm_g, kv_norm_g, w_uq, w_ukv, conv_w,
              spatial_w, spatial_b, w_out, w_router, w_gate, w_up, w_down, final_norm_g):
    rope = axial_rope_tables(x_sample.shape[1], x_sample.dtype)
    xp, xs = x_prompt, x_sample
    ckv_list, kpe_list = [], []
    for l in range(DEPTH):
        p = dict(norm1_g=norm1_g[l], norm2_g=norm2_g[l], w_in=w_in[l], q_norm_g=q_norm_g[l],
                 kv_norm_g=kv_norm_g[l], w_uq=w_uq[l], w_ukv=w_ukv[l], conv_w=conv_w[l],
                 spatial_w=spatial_w[l], spatial_b=spatial_b[l], w_out=w_out[l],
                 w_router=w_router[l], w_gate=w_gate[l], w_up=w_up[l], w_down=w_down[l])
        mod_ctx = (jax.nn.silu(c_ctx) @ w_ada[l] + b_ada[l])[None, None, :]
        xp, ckv, kpe = layer_step(xp, mod_ctx, None, None, None, p)
        ckv_list.append(ckv)
        kpe_list.append(kpe)
        mod_lat = (jax.nn.silu(c) @ w_ada[l] + b_ada[l])[:, None, :]
        xs, _, _ = layer_step(xs, mod_lat, rope, cache_ckv[:, l], cache_krope[:, l], p)
    y_prompt = rmsnorm(xp, final_norm_g)
    y_sample = rmsnorm(xs, final_norm_g)
    new_ckv = jnp.stack(ckv_list, axis=1)
    new_krope = jnp.stack(kpe_list, axis=1)
    return (y_prompt, y_sample, new_ckv, new_krope)


_drawn_inputs = setup_inputs


def setup_inputs(seed=0):
    import zlib

    import numpy as np

    out = dict(_drawn_inputs(seed))
    spreads = {}
    factors = {'cache_ckv': 7.129, 'cache_krope': 8.0, 'norm2_g': 3.54, 'q_norm_g': 8.0}
    for name, (base, spread) in spreads.items():
        noise = np.random.default_rng([zlib.crc32(name.encode()), seed]).standard_normal(out[name].shape)
        drawn = base * np.exp(spread * noise) if base else spread * noise
        out[name] = __import__('jax').numpy.asarray(drawn.astype(out[name].dtype))
    for name, factor in factors.items():
        out[name] = (out[name] * factor).astype(out[name].dtype)
    return out
```

```python
from contextlib import ExitStack

import numpy as np
import concourse.bass as bass
from concourse import mybir

F32 = mybir.dt.float32
U32 = mybir.dt.uint32
ALU = mybir.AluOpType
ACT = mybir.ActivationFunctionType
AX = mybir.AxisListType.X

P = 128
DEPTH, D = 2, 1024
NP, NS, PAST = 256, 1024, 512
T = NP + NS
NT = T // P
PT = NP // P
KD = D // P
HEADS, NOPE, ROPE, VH = 4, 128, 64, 128
QR, KVR = 256, 128
E, FF = 16, 512
CAP_P, CAP_S = 2 * NP // E, 2 * NS // E
SLOTS = CAP_P + CAP_S
EPS = 1e-6
SCALE = float(NOPE + ROPE) ** -0.5
KEYS_S = PAST + NS
KEYS = NP + KEYS_S
CHUNKS = [(0, 512), (512, 512), (1024, 256)]
GROUP_CHUNKS = [(0, 2, 0), (2, 4, 1), (6, 4, 1)]
KEY_CHUNKS = [(0, 512), (512, 512), (1024, 512), (1536, 256)]

W_IN_UNITS = [(0, 448), (448, 512), (960, 512), (1472, 256)]
BLOCKS = [("cq0", 0, 0, 128), ("cq1", 0, 128, 128), ("ckv", 0, 256, 128), ("kpe", 0, 384, 64),
          ("gb0", 1, 0, 128), ("gb1", 1, 128, 128), ("gc0", 1, 256, 128), ("gc1", 1, 384, 128),
          ("xc0", 2, 0, 128), ("xc1", 2, 128, 128), ("u0", 2, 256, 128), ("u1", 2, 384, 128),
          ("v0", 3, 0, 128), ("v1", 3, 128, 128)]
NB = len(BLOCKS)
LANDED = {"in0": (0, 1), "in1": (1, 1), "in2": (2, 1), "in3": (0, 2), "up": (1, 3), "out0": (2, 2), "out1": (0, 3)}
SLOT_DMAS = [19, 19, 18]

ITEMS = []
for _h in range(HEADS):
    ITEMS += [(kind, _h, 0) for kind in ("qn", "qp", "k0", "k1", "v0", "v1")]
    ITEMS += [("s", _h, t) for t in list(range(PT, NT)) + list(range(PT))]
NI = len(ITEMS)
QTILES = [n for n, it in enumerate(ITEMS) if it[0] == "s"]
NQ = len(QTILES)
TAIL = 3


def keys_of(item):
    return (0, NP) if item[2] < PT else (NP, KEYS_S)


def turned_at(n):
    return QTILES.index(n - 2) if n - 2 in QTILES else None


def pair_at(n):
    i = QTILES.index(n - 3) if n - 3 in QTILES else None
    return i // 2 if i is not None and i % 2 else None


ROUND_AT = [0]
for _n in QTILES:
    ROUND_AT.append(ROUND_AT[-1] + -(-keys_of(ITEMS[_n])[1] // 512))
ROUNDS = ROUND_AT[-1]

class Steps:

    def __init__(self, eng, sem):
        self.eng, self.sem, self.n = eng, sem, 0

    def done(self, ins):
        ins.then_inc(self.sem, 1)
        self.n += 1
        self.eng.wait_ge(self.sem, self.n)


def rope_tables():
    rows = NS // 64
    row = np.repeat(np.arange(rows), 64).astype(np.float32)
    col = np.tile(np.arange(64), rows).astype(np.float32)
    nf = ROPE // 4
    inv = np.power(np.float32(10000.0), -np.arange(nf, dtype=np.float32) / np.float32(nf)).astype(np.float32)
    ang = np.concatenate([row[:, None] * inv] * 2 + [col[:, None] * inv] * 2, axis=-1).astype(np.float32)
    sign = np.concatenate([-np.ones(nf), np.ones(nf)] * 2).astype(np.float32)
    return np.cos(ang).T.astype(np.float32), (np.sin(ang) * sign).T.astype(np.float32)


def backbone(nc, x_prompt, x_sample, cache_ckv, cache_krope, c, c_ctx, w_ada, b_ada, norm1_g, norm2_g, w_in,
             q_norm_g, kv_norm_g, w_uq, w_ukv, conv_w, spatial_w, spatial_b, w_out, w_router, w_gate, w_up,
             w_down, final_norm_g, rope_cos, rope_sin, y_prompt, y_sample, new_ckv, new_krope):
    x_dram = nc.dram_tensor("x_dram", (T, D), F32, kind="Internal").ap()
    xn_dram = nc.dram_tensor("xn_dram", (T, D), F32, kind="Internal").ap()
    mod_dram = nc.dram_tensor("mod_dram", (DEPTH, 2, 6 * D), F32, kind="Internal").ap()

    with ExitStack() as ctx:
        def sb(name, shape, dt=F32):
            return ctx.enter_context(nc.sbuf_tensor(name, shape, dt))

        def sem(name):
            return ctx.enter_context(nc.semaphore(name))

        ring = sb("ring", [P, 3, 4096])
        r1 = sb("r1", [P, 10496])
        lat = sb("lat", [P, 6144])
        r2 = sb("r2", [P, 9216])
        mix = sb("mix", [P, KD, T])
        cos = sb("cos", [ROPE, NS])
        sin = sb("sin", [ROPE, NS])
        ident = sb("ident", [P, P])
        ones = sb("ones", [P, P])
        mod_rows = sb("mod_rows", [96, P])
        vec_rows = sb("vec_rows", [25, P])
        mod_t = sb("mod_t", [P, 96])
        vec_t = sb("vec_t", [P, 25])
        scale1 = sb("scale1", [P, 2, KD])
        scale2 = sb("scale2", [P, 2, KD])
        w_r = sb("w_r", [P, KD, E])
        ss = sb("ss", [P, NT])
        ss_act = sb("ss_act", [P, NT])
        eps = sb("eps", [P, 1])
        rms_lat = sb("rms_lat", [P, 2 * NT])
        inv_lat = sb("inv_lat", [P, 2 * NT])
        rstd = sb("rstd", [P, NT])
        stat = sb("stat", [P, 8])
        pmax = sb("pmax", [P, 2])
        nmax = sb("nmax", [P, 2])
        psum_row = sb("psum_row", [P, 2])
        pinv = sb("pinv", [P, 2])
        logit = sb("logit", [P, 2, E])
        idx_f = sb("idx_f", [P, 2, E])
        gate_t = sb("gate_t", [P, 2, E])
        idx_u = sb("idx_u", [P, 2, E + 2], U32)
        gcol = sb("gcol", [P, 2], U32)
        scol = sb("scol", [P, 2], U32)
        top_i = sb("top_i", [E, SLOTS], U32)
        c_rows = sb("c_rows", [16, P])
        c_t = sb("c_t", [P, 16])
        PS = ctx.enter_context(nc.psum_tensor("PS", [P, 8, 512], F32))

        def psum(bank, n, rows=P):
            return PS[0:rows, bank, 0:n]

        def psum_wide(bank, n, rows=P):
            return PS[0:rows, :, :].rearrange("p b n -> p (b n)")[:, bank * 512:bank * 512 + n]

        hT = r1[:, 0:KD * T].rearrange("p (k t) -> p k t", k=KD)
        QN = r1[:, 0:T]
        QPE = r1[0:ROPE, T:2 * T]
        KN = r1[:, 2 * T:2 * T + KEYS]
        V = r1[:, 2 * T + KEYS:2 * T + 2 * KEYS]
        g1 = r1[:, 0:2048].rearrange("p (g d) -> p g d", g=2)
        g2 = r1[:, 2048:4096].rearrange("p (g d) -> p g d", g=2)
        ada_w = [r1[:, 4096 * i:4096 * (i + 1)].rearrange("p (k n) -> p k n", k=KD) for i in range(2)]
        ada_b = [r2[0:1, 512 * i:512 * (i + 1)] for i in range(2)]
        ada_o = r2[0:2, 1024:1024 + 6 * D]

        CQ = lat[:, 0:2560].rearrange("p (k t) -> p k t", k=2)
        CKV = lat[:, 2560:2560 + KEYS]
        KR = lat[0:ROPE, 4352:4352 + KEYS]
        aff = lat[0:E, 0:T]
        top_v = lat[0:E, 1280:1280 + SLOTS]
        top_f = lat[0:E, 1440:1440 + SLOTS]

        XT = [r2[:, D * i:D * (i + 1)] for i in range(4)]
        junk = r2[:, 4096:5120]
        GC = [r2[:, T * i:T * (i + 1)] for i in range(2)]
        XC = [r2[:, T * (2 + i):T * (3 + i)] for i in range(2)]
        VT = [r2[:, 5120:6400], r2[:, 0:T]]
        VTOK = r2[:, 6400:7680].rearrange("p (c d) -> p c d", c=NT)
        SPW = r2[:, 7680:8192].rearrange("p (g q) -> p g q", g=4)
        WST = r2[:, 8192:8704]
        SPB = r2[0:1, 8704:9216]
        raw_ckv = mix[:, 0, 0:512].rearrange("p (t d) -> p t d", t=4)
        raw_kr = mix[:, 0, 512:768].rearrange("p (t d) -> p t d", t=4)
        ctx_out = mix[:, 1, 0:256].rearrange("p (t d) -> p t d", t=2)
        ctx_kr_out = mix[:, 1, 256:384].rearrange("p (t d) -> p t d", t=2)
        SQ = r2[:, 0:2560].rearrange("p (k t) -> p k t", k=2)
        SQK = r2[:, 2560:3840]
        DG = r2[:, 3840:3840 + 2560].rearrange("p (t q) -> p t q", q=P)
        SHUF = r1[0:ROPE, 6144:7168]
        Pr = [r2[:, 1536 * i:1536 * (i + 1)] for i in range(2)]
        PTr = [r2[:, 3072 * (i + 1):3072 * (i + 2)].rearrange("p (k q) -> p k q", k=12) for i in range(2)]
        XD = [r2[:, D * i:D * (i + 1)] for i in range(2)]
        XO = [r2[:, D * (2 + i):D * (3 + i)] for i in range(2)]
        junk_d = r2[:, 4096:5120]
        XN = [r2[:, D * (5 + i):D * (6 + i)] for i in range(2)]
        H2 = [r2[:, D * (7 + i):D * (8 + i)].rearrange("p (k t) -> p k t", k=KD) for i in range(2)]
        XS = [r2[:, 0:D], r2[0:CAP_P, D:2 * D]]
        XST = [r2[:, 2048 + 1280 * i:3328 + 1280 * i].rearrange("p (k s) -> p k s", k=KD) for i in range(2)]
        SG = r2[:, 4608:5248].rearrange("p (b s) -> p b s", b=4)
        HID = r2[:, 5248:5888].rearrange("p (b s) -> p b s", b=4)
        YE = [r2[:, 6144:7168], r2[0:CAP_P, 7168:8192]]

        W_IN = [ring[:, LANDED[f"in{u}"][0], 0:KD * w].rearrange("p (k n) -> p k n", k=KD)
                for u, (_, w) in enumerate(W_IN_UNITS)]
        W_UQ = ring[:, 1, 0:1536].rearrange("p (k n) -> p k n", k=2)
        W_UKV = ring[:, 1, 1536:2560]
        W_OUT = [ring[:, LANDED[f"out{n}"][0], :].rearrange("p (k n) -> p k n", k=KD) for n in range(2)]
        W_G = ring[:, 0, :].rearrange("p (k n) -> p k n", k=KD)
        W_U = ring[:, 1, :].rearrange("p (k n) -> p k n", k=KD)
        W_D = ring[:, 2, :].rearrange("p (k n) -> p k n", k=4)

        consts_landed = sem("consts_landed")
        ident_zero = sem("ident_zero")
        ident_ready = sem("ident_ready")
        c_landed = sem("c_landed")
        c_turned = sem("c_turned")
        c_ready = sem("c_ready")
        ada_landed = [sem(f"ada_landed{i}") for i in range(2)]
        ada_summed = sem("ada_summed")
        ada_copied = sem("ada_copied")
        ada_stored = sem("ada_stored")
        landed = [sem(f"unit_landed{i}") for i in range(3)]
        vec_landed = sem("vec_landed")
        vec_turned = sem("vec_turned")
        vec_ready = sem("vec_ready")
        xt_landed = [sem(f"xt_landed{i}") for i in range(4)]
        ss_ready = sem("ss_ready")
        xn_ready = sem("xn_ready")
        h_turned = sem("h_turned")
        h_ready = sem("h_ready")
        h_ready2 = sem("h_ready2")
        blk_summed = sem("blk_summed")
        blk_copied = sem("blk_copied")
        sp_landed = sem("sp_landed")
        sp_turned = sem("sp_turned")
        sp_ready = sem("sp_ready")
        v_turned = sem("v_turned")
        vtok_ready = sem("vtok_ready")
        spat_summed = sem("spat_summed")
        spat_used = sem("spat_used")
        cache_landed = sem("cache_landed")
        cache_turned = sem("cache_turned")
        cache_ready = sem("cache_ready")
        sq_ready = sem("sq_ready")
        sq_summed = sem("sq_summed")
        lat_ready = sem("lat_ready")
        ctx_turned = sem("ctx_turned")
        ctx_copied = sem("ctx_copied")
        ctx_stored = sem("ctx_stored")
        item_summed = sem("item_summed")
        item_used = sem("item_used")
        qp_ready = sem("qp_ready")
        max_ready = sem("max_ready")
        inv_ready = sem("inv_ready")
        p_ready = sem("p_ready")
        p_turned = sem("p_turned")
        pt_ready = sem("pt_ready")
        o_summed = sem("o_summed")
        o_copied = sem("o_copied")
        g_landed = sem("g_landed")
        xd_landed = [sem(f"xd_landed{i}") for i in range(2)]
        out_summed = sem("out_summed")
        xo_ready = sem("xo_ready")
        ss2_ready = sem("ss2_ready")
        xn2_ready = sem("xn2_ready")
        xo_stored = [sem(f"xo_stored{i}") for i in range(2)]
        xn_stored = [sem(f"xn_stored{i}") for i in range(2)]
        h2_turned = sem("h2_turned")
        h2_ready = sem("h2_ready")
        log_summed = sem("log_summed")
        lmax_ready = sem("lmax_ready")
        lexp_ready = sem("lexp_ready")
        aff_ready = sem("aff_ready")
        aff_turned = sem("aff_turned")
        afft_ready = sem("afft_ready")
        top_ready = sem("top_ready")
        top_turned = sem("top_turned")
        route_ready = sem("route_ready")
        gcol_ready = sem("gcol_ready")
        scol_ready = sem("scol_ready")
        xs_landed = sem("xs_landed")
        xs_turned = sem("xs_turned")
        xst_ready = sem("xst_ready")
        xst_ready2 = sem("xst_ready2")
        gate_summed = sem("gate_summed")
        silu_ready = sem("silu_ready")
        up_summed = sem("up_summed")
        hid_ready = sem("hid_ready")
        down_summed = sem("down_summed")
        ye_ready = sem("ye_ready")
        ye_added = sem("ye_added")
        dve_own = sem("dve_own")
        pool_waited = sem("pool_waited")
        conv_done = sem("conv_done")
        act_own = sem("act_own")
        rms_ready = sem("rms_ready")
        diag_ready = sem("diag_ready")
        inv_spread = sem("inv_spread")
        f_own = sem("f_own")
        fg_landed = sem("fg_landed")
        fx_landed = [sem(f"fx_landed{i}") for i in range(2)]
        fss_ready = sem("fss_ready")
        fy_ready = sem("fy_ready")
        fy_stored = [sem(f"fy_stored{i}") for i in range(2)]

        block = ctx.enter_context(nc.Block())

        def at(layer, per_layer, n):
            return layer * per_layer + n

        x_tiles = x_dram.rearrange("(t p) d -> t p d", p=P)
        xn_tiles = xn_dram.rearrange("(t p) d -> t p d", p=P)
        ada_src = w_ada.rearrange("l (k p) (n f) -> l n p k f", p=P, f=512)
        ada_bsrc = b_ada.rearrange("l (n f) -> l n f", f=512)
        mod_dst = mod_dram.rearrange("l g (n f) -> l n g f", f=512)
        w_in_src = w_in.rearrange("l (k p) n -> l p k n", p=P)
        w_uq_src = w_uq.rearrange("l (k p) n -> l p k n", p=P)
        w_out_src = w_out.rearrange("l (k p) (h n) -> l h p k n", p=P, h=2)
        w_g_src = w_gate.rearrange("l e (k p) n -> l e p k n", p=P)
        w_u_src = w_up.rearrange("l e (k p) n -> l e p k n", p=P)
        w_d_src = w_down.rearrange("l e (k p) n -> l e p k n", p=P)

        @block.sync
        def _(sp):
            sp.dma_start(cos[:, :], rope_cos).then_inc(consts_landed, 16)
            sp.dma_start(sin[:, :], rope_sin).then_inc(consts_landed, 16)
            sp.dma_start(c_rows[0:8, :], c_ctx.rearrange("(k p) -> k p", p=P)).then_inc(c_landed, 16)
            sp.dma_start(c_rows[8:16, :], c.rearrange("b (k p) -> (b k) p", p=P)).then_inc(c_landed, 16)
            for n in range(12 * DEPTH):
                l, s = n // 12, n % 2
                if n >= 2:
                    sp.wait_ge(ada_summed, n - 1)
                sp.dma_start(ada_w[s], ada_src[l, n % 12]).then_inc(ada_landed[s], 16)
                sp.dma_start(ada_b[s], ada_bsrc[l, n % 12:n % 12 + 1, :]).then_inc(ada_landed[s], 16)

            def unit(slot, *pairs):
                for dst, src in pairs:
                    sp.dma_start(dst, src).then_inc(landed[slot], 16)

            for l in range(DEPTH):
                sp.wait_ge(gate_summed, l * E + 1)
                unit(0, (W_IN[0], w_in_src[l, :, :, 0:448]))
                sp.wait_ge(up_summed, l * E + 1)
                unit(1, (W_IN[1], w_in_src[l, :, :, 448:960]))
                sp.wait_ge(down_summed, l * E + 1)
                unit(2, (W_IN[2], w_in_src[l, :, :, 960:1472]))
                sp.wait_ge(blk_summed, at(l, NB, 4))
                unit(0, (W_IN[3], w_in_src[l, :, :, 1472:1728]))
                sp.wait_ge(blk_summed, at(l, NB, 8))
                unit(1, (W_UQ, w_uq_src[l]), (W_UKV, w_ukv[l]))
                sp.wait_ge(blk_summed, at(l, NB, 12))
                unit(2, (W_OUT[0], w_out_src[l, 0]))
                sp.wait_ge(blk_summed, at(l, NB, 14))
                unit(0, (W_OUT[1], w_out_src[l, 1]))
                sp.wait_ge(item_summed, at(l, NI, NI))
                sp.wait_ge(out_summed, at(l, NT, NT))
                with sp.Fori(0, E) as e:
                    sp.wait_ge(gate_summed, l * E + e + 1)
                    unit(0, (W_G, w_g_src[l, e]))
                    sp.wait_ge(up_summed, l * E + e + 1)
                    unit(1, (W_U, w_u_src[l, e]))
                    sp.wait_ge(down_summed, l * E + e + 1)
                    unit(2, (W_D, w_d_src[l, e]))

        @block.gpsimd
        def _(pool):
            pool.memset(ident[:, :], 0.0).then_inc(ident_zero, 1)
            pool.wait_ge(ident_zero, 1)
            pool.affine_select(out=ident[:, :], in_=ident[:, :], compare_op=ALU.not_equal, fill=1.0, base=0,
                               pattern=[[-1, P]], channel_multiplier=1).then_inc(ident_ready, 1)
            pool.memset(ones[:, :], 1.0).then_inc(ident_ready, 1)
            pool.memset(eps[:, :], EPS).then_inc(ident_ready, 1)
            pool.memset(idx_u[:, :, :], 0).then_inc(ident_ready, 1)
            pool.dma_start(x_dram[0:NP, :], x_prompt[0]).then_inc(ye_added, 16)
            pool.dma_start(x_dram[NP:T, :], x_sample[0]).then_inc(ye_added, 16)
            def stand_alone():
                pool.sem_inc(pool_waited, 1)

            for l in range(DEPTH):
                pool.wait_ge(ada_copied, 12 * (l + 1))
                pool.dma_start(mod_dram[l], ada_o).then_inc(ada_stored, 16)
            pool.wait_ge(ada_stored, 16 * DEPTH)

            for l in range(DEPTH):
                pool.wait_ge(ye_added, at(l, 32 * E, 32))
                for dst, src in ((mod_rows[:, :], mod_dram[l].rearrange("g (v p) -> (g v) p", p=P)),
                                 (vec_rows[0:8, :], norm1_g[l].rearrange("(k p) -> k p", p=P)),
                                 (vec_rows[8:16, :], norm2_g[l].rearrange("(k p) -> k p", p=P)),
                                 (vec_rows[16:18, :], q_norm_g[l].rearrange("(k p) -> k p", p=P)),
                                 (vec_rows[18:19, :], kv_norm_g[l].rearrange("(k p) -> k p", p=P)),
                                 (vec_rows[19:25, :], conv_w[l].rearrange("w (k p) -> (w k) p", p=P)),
                                 (w_r[:, :, :], w_router[l].rearrange("(k p) e -> p k e", p=P))):
                    pool.dma_start(dst, src).then_inc(vec_landed, 16)
                for t in range(NT):
                    if t >= 4:
                        pool.wait_ge(h_turned, at(l, 3 * KD, KD if t < 6 else 2 * KD))
                    pool.dma_start(XT[t % 4], x_tiles[t]).then_inc(xt_landed[t % 4], 16)
                for dst, src in ((raw_ckv, cache_ckv[0, l].rearrange("(t p) d -> p t d", p=P)),
                                 (raw_kr, cache_krope[0, l].rearrange("(t p) d -> p t d", p=P))):
                    pool.dma_start(dst, src).then_inc(cache_landed, 16)
                pool.dma_start(SPW, spatial_w[l].rearrange("g p q -> p g q")).then_inc(sp_landed, 16)
                pool.dma_start(SPB, spatial_b[l].rearrange("g p -> (g p)")[None, :]).then_inc(sp_landed, 16)
                pool.wait_ge(ctx_copied, at(l, 1, 1))
                pool.dma_start(new_ckv[0, l].rearrange("(t p) d -> p t d", p=P), ctx_out).then_inc(ctx_stored, 16)
                pool.dma_start(new_krope[0, l].rearrange("(t p) d -> p t d", p=P), ctx_kr_out).then_inc(ctx_stored, 16)
                for i, n in enumerate(QTILES):
                    keys = keys_of(ITEMS[n])[1]
                    pool.wait_ge(inv_ready, at(l, NQ, i + 1))
                    pool.wait_ge(item_used, at(l, NI, n + 1))
                    pool.tensor_scalar(Pr[i % 2][:, 0:keys], Pr[i % 2][:, 0:keys], pinv[:, i % 2:i % 2 + 1], None,
                                       ALU.mult).then_inc(p_ready, 1)
                pool.wait_ge(o_summed, at(l, NQ // 2, NQ // 2))
                for g in range(2):
                    for v, dst in ((2, g1), (5, g2)):
                        pool.dma_start(dst[:, g, :], mod_dram[l, g:g + 1, v * D:(v + 1) * D].to_broadcast([P, D]))\
                            .then_inc(g_landed, 16)

                def load_xd(t):
                    if t >= 2:
                        pool.wait_ge(xo_ready, at(l, NT, t - 1))
                    pool.dma_start(XD[t % 2], x_tiles[t]).then_inc(xd_landed[t % 2], 16)

                load_xd(0)
                load_xd(1)
                for t in range(NT):
                    pool.wait_ge(xo_ready, at(l, NT, t + 1))
                    pool.dma_start(x_tiles[t], XO[t % 2]).then_inc(xo_stored[t % 2], 16)
                    if t + 2 < NT:
                        load_xd(t + 2)
                    pool.wait_ge(xn2_ready, at(l, NT, t + 1))
                    pool.dma_start(xn_tiles[t], XN[t % 2]).then_inc(xn_stored[t % 2], 16)
                for s in range(2):
                    pool.wait_ge(xn_stored[s], at(l, 16 * NT // 2, 16 * NT // 2))
                    pool.wait_ge(xo_stored[s], at(l, 16 * NT // 2, 16 * NT // 2))
                pool.wait_ge(route_ready, at(l, 1, 1))

                def gather(e):
                    for g in range(2):
                        ins = pool.tensor_copy(gcol[:, g:g + 1], idx_u[:, g, bass.ds(e, 1)])
                    ins.then_inc(gcol_ready, 1)
                    pool.wait_ge(gcol_ready, l * (E + 2) + e + 1)
                    stand_alone()
                    pool.indirect_dma_start(XS[0], None, xn_dram, bass.IndirectOffsetOnAxis(gcol[:, 0:1], 0))\
                        .then_inc(xs_landed, 16)
                    pool.indirect_dma_start(XS[1], None, xn_dram,
                                            bass.IndirectOffsetOnAxis(gcol[0:CAP_P, 1:2], 0)).then_inc(xs_landed, 16)

                gather(0)
                pool.wait_ge(xs_turned, l * (E + 1) + 1)
                gather(1)
                with pool.Fori(0, E) as e:
                    pool.wait_ge(xs_turned, l * (E + 1) + e + 2)
                    stand_alone()
                    gather(e + 2)
                    pool.wait_ge(ye_added, l * (32 * E) + e * 32 + 32)
                    stand_alone()
                    for g in range(2):
                        ins = pool.tensor_copy(scol[:, g:g + 1], idx_u[:, g, bass.ds(e, 1)])
                    ins.then_inc(scol_ready, 1)
                    pool.wait_ge(scol_ready, l * E + e + 1)
                    pool.wait_ge(ye_ready, l * E + e + 2)
                    stand_alone()
                    pool.indirect_dma_start(x_dram, bass.IndirectOffsetOnAxis(scol[:, 0:1], 0), YE[0], None,
                                            compute_op=ALU.add).then_inc(ye_added, 16)
                    pool.indirect_dma_start(x_dram, bass.IndirectOffsetOnAxis(scol[0:CAP_P, 1:2], 0), YE[1], None,
                                            compute_op=ALU.add).then_inc(ye_added, 16)
                pool.wait_ge(ye_added, l * (32 * E) + 32 * E + 32)
                pool.wait_ge(xs_landed, (l + 1) * 32 * (E + 2))
                pool.wait_ge(xst_ready, at(l, E + 1, E + 1))
                pool.wait_ge(xst_ready2, at(l, E + 1, E + 1))

            pool.dma_start(g1[:, 0, :], final_norm_g[None, :].to_broadcast([P, D])).then_inc(fg_landed, 16)
            for t in range(2):
                pool.dma_start(XD[t % 2], x_tiles[t]).then_inc(fx_landed[t % 2], 16)
            for t in range(NT):
                pool.wait_ge(fy_ready, t + 1)
                dst = y_prompt[0, t * P:(t + 1) * P, :] if t < PT else y_sample[0, (t - PT) * P:(t - PT + 1) * P, :]
                pool.dma_start(dst, XO[t % 2]).then_inc(fy_stored[t % 2], 16)
                if t + 2 < NT:
                    pool.dma_start(XD[t % 2], x_tiles[t + 2]).then_inc(fx_landed[t % 2], 16)
            for s in range(2):
                pool.wait_ge(fy_stored[s], 16 * NT // 2)
            pool.wait_ge(ctx_stored, 32 * DEPTH)

        @block.tensor
        def _(pe):
            for signal in (gate_summed, up_summed, down_summed):
                pe.sem_inc(signal, 1)
            pe.wait_ge(ident_ready, 4)
            pe.wait_ge(c_landed, 32)
            pe.transpose(psum(7, 16), c_rows[:, :], ident[0:16, 0:16]).then_inc(c_turned, 1)
            pe.wait_ge(c_ready, 1)
            for n in range(12 * DEPTH):
                s = n % 2
                if n >= 2:
                    pe.wait_ge(ada_copied, n - 1)
                pe.wait_ge(ada_landed[s], 32 * (n // 2 + 1))
                for k in range(KD):
                    pe.matmul(psum(s, 512, 2), c_t[:, k:16:KD], ada_w[s][:, k, :], start=(k == 0), stop=False)
                pe.matmul(psum(s, 512, 2), ones[0:1, 0:2], ada_b[s], start=False, stop=True).then_inc(ada_summed, 1)

            def unit_landed(l, name):
                slot, n = LANDED[name]
                pe.wait_ge(landed[slot], l * (16 * SLOT_DMAS[slot]) + 16 * n)

            for l in range(DEPTH):
                pe.wait_ge(vec_landed, at(l, 112, 112))
                pe.transpose(psum(6, 96), mod_rows[:, :], ident[0:96, 0:96]).then_inc(vec_turned, 1)
                pe.transpose(psum(7, 25), vec_rows[:, :], ident[0:25, 0:25]).then_inc(vec_turned, 1)
                n = 0
                for t0, tiles, g in GROUP_CHUNKS:
                    pe.wait_ge(xn_ready, at(l, NT, t0 + tiles))
                    for k in range(KD):
                        if n >= 4:
                            pe.wait_ge(h_ready if n % 2 == 0 else h_ready2, at(l, 12, (n - 4) // 2 + 1))
                        for j in range(tiles):
                            ins = pe.transpose(PS[:, n % 4, j * P:(j + 1) * P], XT[(t0 + j) % 4][:, k * P:(k + 1) * P],
                                               ident[:, :])
                        ins.then_inc(h_turned, 1)
                        n += 1
                pe.wait_ge(cache_landed, at(l, 32, 32))
                pe.wait_ge(vec_ready, at(l, 1, 1))
                for t in range(4):
                    ins = pe.transpose(PS[:, 6, t * P:(t + 1) * P], raw_ckv[:, t, :], ident[:, :])
                ins.then_inc(cache_turned, 1)
                for t in range(4):
                    ins = pe.transpose(PS[0:ROPE, 7, t * P:(t + 1) * P], raw_kr[:, t, :], ident[:, :])
                ins.then_inc(cache_turned, 1)
                pe.wait_ge(h_ready, at(l, 12, 12))
                pe.wait_ge(h_ready2, at(l, 12, 12))
                seen = -1
                for b, (name, u, c0, w) in enumerate(BLOCKS):
                    if u != seen:
                        unit_landed(l, f"in{u}")
                        seen = u
                    if b >= 2:
                        pe.wait_ge(blk_copied, at(l, NB, b - 1))
                    base = 3 * (b % 2)
                    for k in range(KD):
                        for j, (t0, tn) in enumerate(CHUNKS):
                            ins = pe.matmul(psum(base + j, tn, w), W_IN[u][:, k, c0:c0 + w], hT[:, k, t0:t0 + tn],
                                            start=(k == 0), stop=(k == KD - 1))
                    ins.then_inc(blk_summed, 1)
                    if name == "gb1":
                        pe.wait_ge(sp_landed, at(l, 32, 32))
                        pe.wait_ge(cache_ready, at(l, 2, 2))
                        for g in range(4):
                            ins = pe.transpose(PS[:, 6, g * P:(g + 1) * P], SPW[:, g, :], ident[:, :])
                        ins.then_inc(sp_turned, 1)
                for cg in range(2):
                    pe.wait_ge(blk_copied, at(l, NB, NB - 1 + cg))
                    for t in range(NT):
                        ins = pe.transpose(psum_wide(0 if cg == 0 else 3, T)[:, t * P:(t + 1) * P],
                                           VT[cg][:, t * P:(t + 1) * P], ident[:, :])
                    ins.then_inc(v_turned, 1)
                    pe.wait_ge(vtok_ready, at(l, 2, cg + 1))
                    pe.wait_ge(sp_ready, at(l, 1, 1))
                    for t in range(0, NT, 2):
                        m = cg * 5 + t // 2
                        if m >= 2:
                            pe.wait_ge(spat_used, at(l, 10, m - 1))
                        for j in range(2):
                            out = PS[:, 6 + m % 2, j * 256:(j + 1) * 256]
                            pe.matmul(out, VTOK[:, t + j, :], WST[:, cg * 256:(cg + 1) * 256], start=True, stop=False)
                            ins = pe.matmul(out, ones[0:1, :], SPB[:, cg * 256:(cg + 1) * 256], start=False, stop=True)
                        ins.then_inc(spat_summed, 1)
                pe.wait_ge(sq_ready, at(l, 1, 1))
                for t in range(NT):
                    for k in range(2):
                        pe.matmul(PS[:, 0, t:t + 1], SQ[:, k, t * P:(t + 1) * P], ones[:, 0:1], start=(k == 0),
                                  stop=(k == 1))
                    ins = pe.matmul(PS[:, 0, NT + t:NT + t + 1], SQK[:, t * P:(t + 1) * P], ones[:, 0:1], start=True,
                                    stop=True)
                ins.then_inc(sq_summed, 1)
                pe.wait_ge(diag_ready, at(l, 1, 1))
                for q in range(2):
                    for t in range(NT):
                        ins = pe.matmul(psum_wide(3 * q, T)[:, t * P:(t + 1) * P], ones[:, :], DG[:, q * NT + t, :],
                                        start=True, stop=True)
                ins.then_inc(inv_spread, 1)
                pe.wait_ge(lat_ready, at(l, 1, 1))
                for t in range(PT):
                    pe.transpose(PS[:, 6, t * P:(t + 1) * P], CKV[:, t * P:(t + 1) * P], ident[:, :])
                    ins = pe.transpose(PS[:, 6, 256 + t * ROPE:256 + (t + 1) * ROPE], KR[:, t * P:(t + 1) * P],
                                       ident[0:ROPE, 0:ROPE])
                ins.then_inc(ctx_turned, 1)
                pe.wait_ge(ctx_copied, at(l, 1, 1))
                unit_landed(l, "up")

                def parts(n):
                    kind, h, t = ITEMS[n]
                    base = 3 * (n % 2)
                    if kind == "s":
                        k0, keys = keys_of(ITEMS[n])
                        for j in range(0, keys, 512):
                            w = min(512, keys - j)
                            out = psum(base + j // 512, w)
                            pe.matmul(out, QN[:, t * P:(t + 1) * P], KN[:, k0 + j:k0 + j + w], start=True, stop=False)
                            ins = pe.matmul(out, QPE[:, t * P:(t + 1) * P], KR[:, k0 + j:k0 + j + w], start=False,
                                            stop=True)
                            yield ins, j + w == keys
                    elif kind in ("qn", "qp"):
                        c0, w = (h * 192, NOPE) if kind == "qn" else (h * 192 + NOPE, ROPE)
                        for j, (t0, tn) in enumerate(CHUNKS):
                            for k in range(2):
                                ins = pe.matmul(psum(base + j, tn, w), W_UQ[:, k, c0:c0 + w], CQ[:, k, t0:t0 + tn],
                                                start=(k == 0), stop=(k == 1))
                            yield ins, t0 + tn == T
                    elif kind in ("k0", "k1"):
                        for j, (t0, tn) in enumerate(KEY_CHUNKS[0:3] if kind == "k0" else KEY_CHUNKS[3:4]):
                            ins = pe.matmul(psum(base + j, tn), W_UKV[:, h * 256:h * 256 + NOPE], CKV[:, t0:t0 + tn],
                                            start=True, stop=True)
                            yield ins, t0 + tn in (1536, KEYS)
                    else:
                        for j, (t0, tn) in enumerate(KEY_CHUNKS[0:3] if kind == "v0" else KEY_CHUNKS[3:4]):
                            for q in range(tn // P):
                                ins = pe.matmul(PS[:, base + j, q * P:(q + 1) * P],
                                                CKV[:, t0 + q * P:t0 + (q + 1) * P],
                                                W_UKV[:, h * 256 + NOPE:(h + 1) * 256], start=True, stop=True)
                            yield ins, t0 + tn in (1536, KEYS)

                def turns(i):
                    keys = keys_of(ITEMS[QTILES[i]])[1]
                    pe.wait_ge(p_ready, at(l, NQ, i + 1))
                    for r in range(ROUND_AT[i + 1] - ROUND_AT[i]):
                        done = ROUND_AT[i] + r
                        if done:
                            pe.wait_ge(pt_ready, at(l, ROUNDS, done))
                        for j in range(min(4, keys // P - 4 * r)):
                            ins = pe.transpose(PS[:, 6, j * P:(j + 1) * P],
                                               Pr[i % 2][:, (4 * r + j) * P:(4 * r + j + 1) * P], ident[:, :])
                        yield ins.then_inc(p_turned, 1)

                def times_v(pair):
                    k0, keys = keys_of(ITEMS[QTILES[2 * pair]])
                    pe.wait_ge(pt_ready, at(l, ROUNDS, ROUND_AT[2 * pair + 2]))
                    if pair:
                        pe.wait_ge(o_copied, at(l, NQ // 2, pair))
                    for k in range(keys // P):
                        ins = pe.matmul(psum(7, 256), V[:, k0 + k * P:k0 + (k + 1) * P], PTr[pair % 2][:, k, :],
                                        start=(k == 0), stop=(k == keys // P - 1))
                    ins.then_inc(o_summed, 1)

                for n in range(NI + TAIL + 1):
                    if pair_at(n) is not None:
                        times_v(pair_at(n))
                    turning = turns(turned_at(n)) if turned_at(n) is not None else iter(())
                    if n < NI:
                        if n >= 2:
                            pe.wait_ge(item_used, at(l, NI, n - 1))
                        if ITEMS[n][0] == "s" and ITEMS[n - 1][0] != "s":
                            pe.wait_ge(qp_ready, at(l, HEADS, ITEMS[n][1] + 1))
                        for ins, last in parts(n):
                            if last:
                                ins.then_inc(item_summed, 1)
                            next(turning, None)
                    for _ in turning:
                        pass
                unit_landed(l, "out0")
                unit_landed(l, "out1")
                for s in range(NT + 3):
                    if s < NT:
                        if s >= 2:
                            pe.wait_ge(xo_ready, at(l, NT, s - 1))
                        if s == 0:
                            pe.wait_ge(o_copied, at(l, NQ // 2, NQ // 2))
                        for n in range(2):
                            for k in range(KD):
                                ins = pe.matmul(psum(2 * (s % 2) + n, 512), mix[:, k, s * P:(s + 1) * P],
                                                W_OUT[n][:, k, :], start=(k == 0), stop=(k == KD - 1))
                        ins.then_inc(out_summed, 1)
                    t = s - 1
                    if 0 <= t < NT:
                        pe.wait_ge(xn2_ready, at(l, NT, t + 1))
                        if t >= 1:
                            pe.wait_ge(h2_ready, at(l, 2 * NT, 2 * t))
                        for k in range(KD):
                            ins = pe.transpose(PS[:, 4 + k // 4, (k % 4) * P:(k % 4 + 1) * P],
                                               XN[t % 2][:, k * P:(k + 1) * P], ident[:, :])
                        ins.then_inc(h2_turned, 1)
                    t = s - 2
                    if 0 <= t < NT:
                        pe.wait_ge(h2_ready, at(l, 2 * NT, 2 * (t + 1)))
                        if t >= 1:
                            pe.wait_ge(lexp_ready, at(l, NT, t))
                        for k in range(KD):
                            ins = pe.matmul(psum(6, E), H2[t % 2][:, k, :], w_r[:, k, :], start=(k == 0),
                                            stop=(k == KD - 1))
                        ins.then_inc(log_summed, 1)
                    t = s - 3
                    if 0 <= t < NT:
                        pe.wait_ge(aff_ready, at(l, NT, t + 1))
                        if t >= 1:
                            pe.wait_ge(afft_ready, at(l, NT, t))
                        pe.transpose(psum(7, P, E), logit[:, t % 2, :], ident[:, :]).then_inc(aff_turned, 1)
                pe.wait_ge(top_ready, at(l, 1, 1))
                for q, src in enumerate((top_f, top_v)):
                    pe.transpose(PS[:, 5, q * 64:q * 64 + E], src[:, CAP_P:SLOTS], ident[0:E, 0:E])
                    ins = pe.transpose(PS[0:CAP_P, 5, q * 64 + E:q * 64 + 2 * E], src[:, 0:CAP_P], ident[0:E, 0:E])
                ins.then_inc(top_turned, 1)
                pe.wait_ge(route_ready, at(l, 1, 1))

                def turn_rows(n):
                    pe.wait_ge(xs_landed, l * (32 * (E + 2)) + n * 32 + 32)
                    for k in range(KD):
                        out = PS[:, 4 + k // 2, (k % 2) * 256:(k % 2) * 256 + SLOTS]
                        pe.transpose(out[:, 0:P], XS[0][:, k * P:(k + 1) * P], ident[:, :])
                        ins = pe.transpose(out[:, P:SLOTS], XS[1][:, k * P:(k + 1) * P], ident[0:CAP_P, 0:CAP_P])
                    ins.then_inc(xs_turned, 1)

                turn_rows(0)
                with pe.Fori(0, E // 2) as ee:
                    for par in range(2):
                        e = ee * 2 + par
                        pe.wait_ge(xst_ready, l * (E + 1) + e + 1)
                        pe.wait_ge(xst_ready2, l * (E + 1) + e + 1)
                        for slot, first, w, base, signal in ((0, 3, W_G, 0, gate_summed), (1, 3, W_U, 2, up_summed)):
                            pe.wait_ge(landed[slot], l * (16 * SLOT_DMAS[slot]) + e * 16 + 16 * (first + 1))
                            for b in range(4):
                                for k in range(KD):
                                    ins = pe.matmul(PS[:, base + b // 2, (b % 2) * 256:(b % 2) * 256 + SLOTS],
                                                    w[:, k, b * P:(b + 1) * P], XST[par][:, k, :], start=(k == 0),
                                                    stop=(k == KD - 1))
                            ins.then_inc(signal, 1)
                            if slot == 0:
                                pe.wait_ge(ye_ready, l * E + e + 1)
                                turn_rows(e + 1)
                        pe.wait_ge(landed[2], l * (16 * SLOT_DMAS[2]) + e * 16 + 48)
                        pe.wait_ge(hid_ready, l * E + e + 1)
                        pe.wait_ge(xst_ready, l * (E + 1) + e + 2)
                        pe.wait_ge(xst_ready2, l * (E + 1) + e + 2)
                        for base, m, s0 in ((4, P, 0), (6, CAP_P, P)):
                            for n in range(2):
                                for k in range(4):
                                    ins = pe.matmul(psum(base + n, 512, m), HID[:, k, s0:s0 + m],
                                                    W_D[:, k, n * 512:(n + 1) * 512], start=(k == 0), stop=(k == 3))
                        ins.then_inc(down_summed, 1)

        @block.scalar
        def _(act):
            act.wait_ge(c_turned, 1)
            act.activation(c_t[:, :], psum(7, 16), ACT.Silu).then_inc(c_ready, 1)
            for n in range(12 * DEPTH):
                act.wait_ge(ada_summed, n + 1)
                if n == 12:
                    act.wait_ge(ada_stored, 16)
                act.activation(ada_o[:, 512 * (n % 12):512 * (n % 12 + 1)], psum(n % 2, 512, 2), ACT.Copy)\
                    .then_inc(ada_copied, 1)

            own = Steps(act, act_own)
            act.wait_ge(ident_ready, 4)
            for l in range(DEPTH):
                def root_mean_square(dst, src, scratch, t):
                    own.done(act.activation(scratch, src, ACT.Square, accum_out=ss_act[:, t:t + 1]))
                    return act.activation(dst, ss_act[:, t:t + 1], ACT.Sqrt, bias=eps[:, :], scale=1.0 / D)

                def xt_landed_at(t):
                    uses = (3, 3, 2, 2)[t % 4]
                    act.wait_ge(xt_landed[t % 4], at(l, 16 * uses, 16 * (t // 4 + 1)))

                n = 0
                for t0, tiles, g in GROUP_CHUNKS:
                    for t in range(t0, t0 + tiles):
                        xt_landed_at(t)
                        root_mean_square(ss[:, t:t + 1], XT[t % 4], junk, t).then_inc(ss_ready, 1)
                    act.wait_ge(vec_ready, at(l, 1, 1))
                    for k in range(KD):
                        if n % 2 == 0:
                            act.wait_ge(h_turned, at(l, 3 * KD, n + 1))
                            act.activation(hT[:, k, t0 * P:(t0 + tiles) * P], psum(n % 4, tiles * P), ACT.Identity,
                                           bias=mod_t[:, g * 48 + k:g * 48 + k + 1],
                                           scale=scale1[:, g, k:k + 1]).then_inc(h_ready, 1)
                        n += 1
                act.wait_ge(cache_turned, at(l, 2, 2))
                act.activation(CKV[:, NP:NP + PAST], psum(6, 512), ACT.Copy).then_inc(cache_ready, 1)
                act.activation(KR[:, NP:NP + PAST], psum(7, 512, ROPE), ACT.Copy).then_inc(cache_ready, 1)
                for b, (name, u, c0, w) in enumerate(BLOCKS):
                    base = 3 * (b % 2)
                    act.wait_ge(blk_summed, at(l, NB, b + 1))
                    if name in ("ckv", "kpe"):
                        dst = CKV if name == "ckv" else KR
                        act.activation(dst[:, 0:NP], psum(base, NP, w), ACT.Copy)
                        act.activation(dst[:, NP + PAST:KEYS], psum_wide(base, T, w)[:, NP:T], ACT.Copy)\
                            .then_inc(blk_copied, 1)
                    else:
                        dst = {"cq0": CQ[:, 0, :], "cq1": CQ[:, 1, :], "gb0": mix[:, 4, :], "gb1": mix[:, 5, :],
                               "gc0": GC[0], "gc1": GC[1], "xc0": XC[0], "xc1": XC[1], "u0": mix[:, 6, :],
                               "u1": mix[:, 7, :], "v0": VT[0], "v1": VT[1]}[name]
                        if name == "v1":
                            act.wait_ge(conv_done, at(l, 1, 1))
                        act.activation(dst, psum_wide(base, T, w), ACT.Copy).then_inc(blk_copied, 1)
                    if name == "gc0":
                        act.wait_ge(sp_turned, at(l, 1, 1))
                        act.activation(WST, psum(6, 512), ACT.Copy).then_inc(sp_ready, 1)
                for cg in range(2):
                    act.wait_ge(v_turned, at(l, 2, cg + 1))
                    if cg:
                        act.wait_ge(spat_summed, at(l, 10, 5))
                    act.activation(VTOK.rearrange("p c d -> p (c d)"), psum_wide(3 * cg, T), ACT.Copy)\
                        .then_inc(vtok_ready, 1)
                act.wait_ge(sq_summed, at(l, 1, 1))
                act.activation(rms_lat[:, 0:NT], PS[:, 0, 0:NT], ACT.Sqrt, bias=eps[:, :], scale=1.0 / QR)
                act.activation(rms_lat[:, NT:2 * NT], PS[:, 0, NT:2 * NT], ACT.Sqrt, bias=eps[:, :],
                               scale=1.0 / KVR).then_inc(rms_ready, 1)
                act.wait_ge(ctx_turned, at(l, 1, 1))
                act.activation(ctx_out.rearrange("p t d -> p (t d)"), psum(6, 256), ACT.Copy)
                act.activation(ctx_kr_out.rearrange("p t d -> p (t d)"), PS[:, 6, 256:384], ACT.Copy)\
                    .then_inc(ctx_copied, 1)
                for n in range(NI + TAIL + 1):
                    pair = pair_at(n)
                    if pair is not None:
                        _, h, t = ITEMS[QTILES[2 * pair]]
                        if pair == 5:
                            act.wait_ge(ctx_stored, at(l, 32, 32))
                        act.wait_ge(o_summed, at(l, NQ // 2, pair + 1))
                        act.activation(mix[:, h, t * P:(t + 2) * P], psum(7, 256), ACT.Copy).then_inc(o_copied, 1)
                    if n >= NI:
                        continue
                    kind, h, t = ITEMS[n]
                    base = 3 * (n % 2)
                    if kind == "s":
                        i = QTILES.index(n)
                        keys = keys_of(ITEMS[n])[1]
                        act.wait_ge(max_ready, at(l, NQ, i + 1))
                        if i >= 2:
                            act.wait_ge(p_turned, at(l, ROUNDS, ROUND_AT[i - 1]))
                        act.activation(Pr[i % 2][:, 0:keys], psum_wide(base, keys), ACT.Exp,
                                       bias=nmax[:, i % 2:i % 2 + 1], scale=SCALE,
                                       accum_out=psum_row[:, i % 2:i % 2 + 1]).then_inc(item_used, 1)
                    else:
                        act.wait_ge(item_summed, at(l, NI, n + 1))
                        dst, w = {"qn": (QN, T), "qp": (QPE, T), "k0": (KN[:, 0:1536], 1536),
                                  "k1": (KN[:, 1536:KEYS], 256), "v0": (V[:, 0:1536], 1536),
                                  "v1": (V[:, 1536:KEYS], 256)}[kind]
                        rows = ROPE if kind == "qp" else P
                        act.activation(dst, psum_wide(base, w, rows), ACT.Copy).then_inc(item_used, 1)
                for s in range(NT + 3):
                    if s < NT:
                        act.wait_ge(xo_ready, at(l, NT, s + 1))
                        root_mean_square(ss[:, s:s + 1], XO[s % 2], junk_d, s).then_inc(ss2_ready, 1)
                    t = s - 1
                    if 0 <= t < NT:
                        g = 0 if t < PT else 1
                        act.wait_ge(h2_turned, at(l, NT, t + 1))
                        if t >= 2:
                            act.wait_ge(log_summed, at(l, NT, t - 1))
                        for k in range(KD // 2):
                            ins = act.activation(H2[t % 2][:, k, :], PS[:, 4 + k // 4, (k % 4) * P:(k % 4 + 1) * P],
                                                 ACT.Identity, bias=mod_t[:, g * 48 + 24 + k:g * 48 + 25 + k],
                                                 scale=scale2[:, g, k:k + 1])
                        ins.then_inc(h2_ready, 1)
                    t = s - 2
                    if 0 <= t < NT:
                        act.wait_ge(lmax_ready, at(l, NT, t + 1))
                        if t >= 2:
                            act.wait_ge(aff_turned, at(l, NT, t - 1))
                        act.activation(logit[:, t % 2, :], psum(6, E), ACT.Exp, bias=nmax[:, t % 2:t % 2 + 1],
                                       accum_out=psum_row[:, t % 2:t % 2 + 1]).then_inc(lexp_ready, 1)
                    t = s - 3
                    if 0 <= t < NT:
                        act.wait_ge(aff_turned, at(l, NT, t + 1))
                        act.activation(aff[:, t * P:(t + 1) * P], psum(7, P, E), ACT.Copy).then_inc(afft_ready, 1)

                def modulate_rows(n, par):
                    act.wait_ge(xs_turned, l * (E + 1) + n + 1)
                    for k in range(KD // 2):
                        for g, s0, m in ((1, 0, CAP_S), (0, CAP_S, CAP_P)):
                            c0 = (k % 2) * 256 + s0
                            ins = act.activation(XST[par][:, k, s0:s0 + m], PS[:, 4 + k // 2, c0:c0 + m], ACT.Identity,
                                                 bias=mod_t[:, g * 48 + 24 + k:g * 48 + 25 + k],
                                                 scale=scale2[:, g, k:k + 1])
                    ins.then_inc(xst_ready, 1)

                modulate_rows(0, 0)
                with act.Fori(0, E // 2) as ee:
                    for par in range(2):
                        e = ee * 2 + par
                        act.wait_ge(gate_summed, l * E + e + 2)
                        for b in range(2):
                            src = PS[:, b, :].rearrange("p (b s) -> p b s", b=2)[:, :, 0:SLOTS]
                            ins = act.activation(SG[:, 2 * b:2 * b + 2, :], src, ACT.Silu)
                        ins.then_inc(silu_ready, 1)
                        modulate_rows(e + 1, 1 - par)


            for t in range(NT):
                act.wait_ge(fx_landed[t % 2], 16 * (t // 2 + 1))
                own.done(act.activation(junk_d, XD[t % 2], ACT.Square, accum_out=ss_act[:, t:t + 1]))
                act.activation(ss[:, t:t + 1], ss_act[:, t:t + 1], ACT.Sqrt, bias=eps[:, :], scale=1.0 / D)\
                    .then_inc(fss_ready, 1)

        @block.vector
        def _(dve):
            own = Steps(dve, dve_own)
            dve.sem_inc(ye_ready, 1)
            for l in range(DEPTH):
                def step(ins):
                    own.done(ins)

                dve.wait_ge(vec_turned, at(l, 2, 2))
                step(dve.tensor_copy(mod_t[:, :], psum(6, 96)))
                step(dve.tensor_copy(vec_t[:, :], psum(7, 25)))
                for g in range(2):
                    for scale, v, gain in ((scale1, 1, 0), (scale2, 4, 8)):
                        ins = dve.scalar_tensor_tensor(out=scale[:, g, :], in0=mod_t[:, g * 48 + v * 8:g * 48 + v * 8 + 8],
                                                       scalar=1.0, in1=vec_t[:, gain:gain + 8], op0=ALU.add,
                                                       op1=ALU.mult)
                ins.then_inc(vec_ready, 1)
                dve.wait_ge(vec_ready, at(l, 1, 1))
                n = 0
                for t0, tiles, g in GROUP_CHUNKS:
                    for t in range(t0, t0 + tiles):
                        dve.wait_ge(ss_ready, at(l, NT, t + 1))
                        step(dve.reciprocal(rstd[:, t:t + 1], ss[:, t:t + 1]))
                        dve.tensor_scalar(XT[t % 4], XT[t % 4], rstd[:, t:t + 1], None, ALU.mult).then_inc(xn_ready, 1)
                    for k in range(KD):
                        if n % 2 == 1:
                            dve.wait_ge(h_turned, at(l, 3 * KD, n + 1))
                            dve.tensor_scalar(hT[:, k, t0 * P:(t0 + tiles) * P], psum(n % 4, tiles * P),
                                              scale1[:, g, k:k + 1], mod_t[:, g * 48 + k:g * 48 + k + 1], ALU.mult,
                                              ALU.add).then_inc(h_ready2, 1)
                        n += 1
                names = [b[0] for b in BLOCKS]
                for cg in range(2):
                    dve.wait_ge(blk_copied, at(l, NB, names.index(f"xc{cg}") + 1))
                    z, y, gb = GC[cg], XC[cg], mix[:, 4 + cg, :]
                    w = [vec_t[:, 19 + 2 * i + cg:20 + 2 * i + cg] for i in range(3)]
                    step(dve.tensor_tensor(z, z, y, ALU.mult))
                    step(dve.tensor_scalar(y, z, w[1], None, ALU.mult))
                    for a, b in ((0, NP), (NP, T)):
                        ins = dve.scalar_tensor_tensor(out=y[:, a + 1:b], in0=z[:, a:b - 1], scalar=w[0],
                                                       in1=y[:, a + 1:b], op0=ALU.mult, op1=ALU.add)
                    step(ins)
                    for a, b in ((0, NP), (NP, T)):
                        ins = dve.scalar_tensor_tensor(out=y[:, a:b - 1], in0=z[:, a + 1:b], scalar=w[2],
                                                       in1=y[:, a:b - 1], op0=ALU.mult, op1=ALU.add)
                    step(ins)
                    ins = dve.tensor_tensor(gb, gb, y, ALU.mult)
                ins.then_inc(conv_done, 1)
                for cg in range(2):
                    u = mix[:, 6 + cg, :].rearrange("p (t q) -> p t q", q=P)
                    for t in range(0, NT, 2):
                        m = cg * 5 + t // 2
                        dve.wait_ge(spat_summed, at(l, 10, m + 1))
                        src = PS[:, 6 + m % 2, :].rearrange("p (t g q) -> p t g q", t=2, g=2)
                        for half in range(2):
                            r = slice(64 * half, 64 * half + 64)
                            ins = dve.tensor_tensor(u[r, t:t + 2, :], u[r, t:t + 2, :], src[r, :, half, :], ALU.mult)
                        ins.then_inc(spat_used, 1)
                dve.tensor_tensor(SQ, CQ, CQ, ALU.mult)
                dve.tensor_tensor(SQK[:, 0:NP], CKV[:, 0:NP], CKV[:, 0:NP], ALU.mult)
                dve.tensor_tensor(SQK[:, NP:T], CKV[:, NP + PAST:KEYS], CKV[:, NP + PAST:KEYS], ALU.mult)\
                    .then_inc(sq_ready, 1)
                dve.wait_ge(rms_ready, at(l, 1, 1))
                step(dve.reciprocal(inv_lat[:, :], rms_lat[:, :]))
                for t in range(2 * NT):
                    ins = dve.tensor_scalar(DG[:, t, :], ident[:, :], inv_lat[:, t:t + 1], None, ALU.mult)
                ins.then_inc(diag_ready, 1)
                dve.wait_ge(inv_spread, at(l, 1, 1))
                for k in range(2):
                    dve.scalar_tensor_tensor(out=CQ[:, k, :], in0=CQ[:, k, :], scalar=vec_t[:, 16 + k:17 + k], in1=psum_wide(0, T),
                                             op0=ALU.mult, op1=ALU.mult)
                for a, b, o in ((0, NP, 0), (NP, T, PAST)):
                    ins = dve.scalar_tensor_tensor(out=CKV[:, a + o:b + o], in0=CKV[:, a + o:b + o],
                                                   scalar=vec_t[:, 18:19], in1=psum_wide(3, T)[:, a:b], op0=ALU.mult,
                                                   op1=ALU.mult)

                def rotate(x):
                    step(dve.stream_shuffle(SHUF, x, [(i + 16) % 32 for i in range(32)]))
                    step(dve.tensor_tensor(SHUF, SHUF, sin[:, :], ALU.mult))
                    step(dve.tensor_tensor(x, x, cos[:, :], ALU.mult))
                    return dve.tensor_tensor(x, x, SHUF, ALU.add)

                dve.wait_ge(consts_landed, 32)
                step(ins)
                rotate(KR[:, NP + PAST:KEYS]).then_inc(lat_ready, 1)

                for n in range(NI + TAIL + 1):
                    i = turned_at(n)
                    if i is not None:
                        keys = keys_of(ITEMS[QTILES[i]])[1]
                        for r in range(ROUND_AT[i + 1] - ROUND_AT[i]):
                            m = min(4, keys // P - 4 * r)
                            dve.wait_ge(p_turned, at(l, ROUNDS, ROUND_AT[i] + r + 1))
                            dve.tensor_copy(PTr[(i // 2) % 2][:, 4 * r:4 * r + m, (i % 2) * P:(i % 2 + 1) * P],
                                            psum(6, m * P).rearrange("p (k q) -> p k q", q=P)).then_inc(pt_ready, 1)
                    if n >= NI:
                        continue
                    kind, h, t = ITEMS[n]
                    if kind == "qp":
                        dve.wait_ge(item_used, at(l, NI, n + 1))
                        rotate(QPE[:, NP:T]).then_inc(qp_ready, 1)
                    if kind == "s":
                        i = QTILES.index(n)
                        keys = keys_of(ITEMS[n])[1]
                        dve.wait_ge(item_summed, at(l, NI, n + 1))
                        step(dve.tensor_reduce(pmax[:, i % 2:i % 2 + 1], psum_wide(3 * (n % 2), keys), AX, ALU.max))
                        dve.tensor_scalar(nmax[:, i % 2:i % 2 + 1], pmax[:, i % 2:i % 2 + 1], -SCALE, None,
                                          ALU.mult).then_inc(max_ready, 1)
                        dve.wait_ge(item_used, at(l, NI, n + 1))
                        if i >= 2:
                            dve.wait_ge(p_ready, at(l, NQ, i - 1))
                        dve.reciprocal(pinv[:, i % 2:i % 2 + 1], psum_row[:, i % 2:i % 2 + 1]).then_inc(inv_ready, 1)
                dve.wait_ge(g_landed, at(l, 64, 64))
                for s in range(NT + 3):
                    if s < NT:
                        g = 0 if s < PT else 1
                        dve.wait_ge(out_summed, at(l, NT, s + 1))
                        dve.wait_ge(xd_landed[s % 2], at(l, 16 * NT // 2, 16 * (s // 2 + 1)))
                        if s >= 2:
                            dve.wait_ge(xo_stored[s % 2], at(l, 16 * NT // 2, 16 * (s // 2)))
                            dve.wait_ge(ss2_ready, at(l, NT, s - 1))
                        step(dve.tensor_tensor(XO[s % 2], psum_wide(2 * (s % 2), D), g1[:, g, :], ALU.mult))
                        dve.tensor_tensor(XO[s % 2], XO[s % 2], XD[s % 2], ALU.add).then_inc(xo_ready, 1)
                        dve.wait_ge(ss2_ready, at(l, NT, s + 1))
                        step(dve.reciprocal(rstd[:, s:s + 1], ss[:, s:s + 1]))
                        if s >= 2:
                            dve.wait_ge(xn_stored[s % 2], at(l, 16 * NT // 2, 16 * (s // 2)))
                            dve.wait_ge(h2_turned, at(l, NT, s - 1))
                        dve.tensor_scalar(XN[s % 2], XO[s % 2], rstd[:, s:s + 1], None, ALU.mult).then_inc(xn2_ready, 1)
                    t = s - 1
                    if 0 <= t < NT:
                        g = 0 if t < PT else 1
                        dve.wait_ge(h2_turned, at(l, NT, t + 1))
                        if t >= 2:
                            dve.wait_ge(log_summed, at(l, NT, t - 1))
                        for k in range(KD // 2, KD):
                            ins = dve.tensor_scalar(H2[t % 2][:, k, :], PS[:, 4 + k // 4, (k % 4) * P:(k % 4 + 1) * P],
                                                    scale2[:, g, k:k + 1], mod_t[:, g * 48 + 24 + k:g * 48 + 25 + k],
                                                    ALU.mult, ALU.add)
                        ins.then_inc(h2_ready, 1)
                    t = s - 2
                    if 0 <= t < NT:
                        dve.wait_ge(log_summed, at(l, NT, t + 1))
                        step(dve.tensor_reduce(pmax[:, t % 2:t % 2 + 1], psum(6, E), AX, ALU.max))
                        dve.tensor_scalar(nmax[:, t % 2:t % 2 + 1], pmax[:, t % 2:t % 2 + 1], -1.0, None,
                                          ALU.mult).then_inc(lmax_ready, 1)
                        dve.wait_ge(lexp_ready, at(l, NT, t + 1))
                        step(dve.reciprocal(pinv[:, t % 2:t % 2 + 1], psum_row[:, t % 2:t % 2 + 1]))
                        dve.tensor_scalar(logit[:, t % 2, :], logit[:, t % 2, :], pinv[:, t % 2:t % 2 + 1], None,
                                          ALU.mult).then_inc(aff_ready, 1)
                dve.wait_ge(afft_ready, at(l, NT, NT))
                for first, n, slot0, cap in ((0, NP, 0, CAP_P), (NP, NS, CAP_P, CAP_S)):
                    a = aff[:, first:first + n]
                    for j in range(slot0, slot0 + cap, 8):
                        step(dve.max(top_v[:, j:j + 8], a))
                        step(dve.max_index(top_i[:, j:j + 8], top_v[:, j:j + 8], a))
                        step(dve.match_replace(a, top_v[:, j:j + 8], a, -1.0))
                dve.tensor_scalar(top_f[:, 0:CAP_P], top_i[:, 0:CAP_P], 0.0, None, ALU.add)
                dve.tensor_scalar(top_f[:, CAP_P:SLOTS], top_i[:, CAP_P:SLOTS], float(NP), None, ALU.add)\
                    .then_inc(top_ready, 1)
                dve.wait_ge(top_turned, at(l, 1, 1))
                dve.tensor_copy(idx_u[:, 0, 0:E], PS[:, 5, 0:E])
                dve.tensor_copy(idx_u[0:CAP_P, 1, 0:E], PS[0:CAP_P, 5, E:2 * E])
                dve.tensor_copy(gate_t[:, 0, :], PS[:, 5, 64:64 + E])
                dve.tensor_copy(gate_t[0:CAP_P, 1, :], PS[0:CAP_P, 5, 64 + E:64 + 2 * E]).then_inc(route_ready, 1)
                dve.wait_ge(route_ready, at(l, 1, 1))

                def modulate_rows(n, par):
                    dve.wait_ge(xs_turned, l * (E + 1) + n + 1)
                    for k in range(KD // 2, KD):
                        for g, s0, m in ((1, 0, CAP_S), (0, CAP_S, CAP_P)):
                            c0 = (k % 2) * 256 + s0
                            ins = dve.tensor_scalar(XST[par][:, k, s0:s0 + m], PS[:, 4 + k // 2, c0:c0 + m],
                                                    scale2[:, g, k:k + 1],
                                                    mod_t[:, g * 48 + 24 + k:g * 48 + 25 + k], ALU.mult, ALU.add)
                    ins.then_inc(xst_ready2, 1)

                modulate_rows(0, 0)
                with dve.Fori(0, E // 2) as ee:
                    for par in range(2):
                        e = ee * 2 + par
                        modulate_rows(e + 1, 1 - par)
                        dve.wait_ge(up_summed, l * E + e + 2)
                        dve.wait_ge(silu_ready, l * E + e + 1)
                        for b in range(2):
                            src = PS[:, 2 + b, :].rearrange("p (b s) -> p b s", b=2)[:, :, 0:SLOTS]
                            ins = dve.tensor_tensor(HID[:, 2 * b:2 * b + 2, :], SG[:, 2 * b:2 * b + 2, :], src,
                                                    ALU.mult)
                        ins.then_inc(hid_ready, 1)
                        dve.wait_ge(down_summed, l * E + e + 2)
                        dve.wait_ge(ye_added, l * (32 * E) + e * 32 + 32)
                        for q, (base, m) in enumerate(((4, P), (6, CAP_P))):
                            ins = dve.scalar_tensor_tensor(out=YE[q], in0=psum_wide(base, D, m),
                                                           scalar=gate_t[0:m, q, bass.ds(e, 1)], in1=g2[0:m, 1 - q, :],
                                                           op0=ALU.mult, op1=ALU.mult)
                        ins.then_inc(ye_ready, 1)

            dve.wait_ge(fg_landed, 16)
            for t in range(NT):
                dve.wait_ge(fx_landed[t % 2], 16 * (t // 2 + 1))
                dve.wait_ge(fss_ready, t + 1)
                dve.reciprocal(rstd[:, t:t + 1], ss[:, t:t + 1]).then_inc(f_own, 1)
                dve.wait_ge(f_own, t + 1)
                if t >= 2:
                    dve.wait_ge(fy_stored[t % 2], 16 * (t // 2))
                dve.scalar_tensor_tensor(out=XO[t % 2], in0=XD[t % 2], scalar=rstd[:, t:t + 1], in1=g1[:, 0, :],
                                         op0=ALU.mult, op1=ALU.mult).then_inc(fy_ready, 1)


_INS = ["x_prompt", "x_sample", "cache_ckv", "cache_krope", "c", "c_ctx", "w_ada", "b_ada", "norm1_g", "norm2_g",
        "w_in", "q_norm_g", "kv_norm_g", "w_uq", "w_ukv", "conv_w", "spatial_w", "spatial_b", "w_out", "w_router",
        "w_gate", "w_up", "w_down", "final_norm_g"]
_OUTS = [((1, NP, D), "float32"), ((1, NS, D), "float32"), ((1, DEPTH, NP, KVR), "float32"),
         ((1, DEPTH, NP, ROPE), "float32")]


def kernel(**inputs):
    import concourse.bacc as _bacc
    from concourse.bass_utils import run_bass_kernel_spmd as _run

    nc = _bacc.Bacc("TRN2", target_bir_lowering=False, num_devices=1)
    arrays, args = {}, []
    held = {name: np.ascontiguousarray(inputs[name]) for name in _INS}
    held["rope_cos"], held["rope_sin"] = rope_tables()
    for name, a in held.items():
        a = np.ascontiguousarray(a)
        arrays[f"in_{name}_dram"] = a
        args.append(nc.dram_tensor(f"in_{name}_dram", a.shape, mybir.dt.from_np(a.dtype), kind="ExternalInput").ap())
    for i, (shape, dtype) in enumerate(_OUTS):
        args.append(nc.dram_tensor(f"out_{i}_dram", shape, mybir.dt.from_np(np.dtype(dtype)),
                                   kind="ExternalOutput").ap())
    backbone(nc, *args)
    r = _run(nc, [arrays], core_ids=[0])
    return tuple(r.results[0][f"out_{i}_dram"] for i in range(len(_OUTS)))
```
